# Optimizing a Trainium2 kernel written in Bass

```python
import jax, jax.numpy as jnp
from jax import lax
import numpy as np

D_MODEL = 1024
BATCH = 1
SEQ = 512
DEPTH = 1

N_ATTN_HEADS = 8
ATTN_HEAD_DIM = 64
ATTN_WIDTH = N_ATTN_HEADS * ATTN_HEAD_DIM
Q_BLOCK = 128
FORGET_BIAS_OFFSET = 3.0
N_SGU_GROUPS = 8
SGU_GROUP_DIM = 64
SGU_WIDTH = N_SGU_GROUPS * SGU_GROUP_DIM
CHUNK = 128
N_BRANCHES = 2
D_FF = 2816
RMS_EPS = 1e-6
LN_EPS = 1e-5

IN_SIZES = (ATTN_WIDTH, ATTN_WIDTH, ATTN_WIDTH, N_ATTN_HEADS, SGU_WIDTH, SGU_WIDTH, N_BRANCHES * D_MODEL)
IN_WIDTH = sum(IN_SIZES)
SPLIT_POINTS = tuple(sum(IN_SIZES[:i + 1]) for i in range(len(IN_SIZES) - 1))

kernel_name = "macaron_fox_sgu_gated_hybrid"

def rms_norm(x, gain):
    x32 = x.astype(jnp.float32)
    y = x32 * lax.rsqrt(jnp.mean(x32 * x32, axis=-1, keepdims=True) + RMS_EPS)
    return y.astype(x.dtype) * gain

def layer_norm(x, gain, bias):
    x32 = x.astype(jnp.float32)
    mu = jnp.mean(x32, axis=-1, keepdims=True)
    var = jnp.mean(jnp.square(x32 - mu), axis=-1, keepdims=True)
    y = (x32 - mu) * lax.rsqrt(var + LN_EPS)
    return y.astype(x.dtype) * gain + bias

def swiglu(x, w_in, w_out):
    gate, up = jnp.split(x @ w_in, 2, axis=-1)
    return (jax.nn.silu(gate) * up) @ w_out

def forgetting_attention(q, k, v, f_logit):
    B, S, H, dh = q.shape
    nb = S // Q_BLOCK
    log_f = jax.nn.log_sigmoid(f_logit.astype(jnp.float32))
    c = jnp.cumsum(log_f, axis=1).transpose(0, 2, 1)
    qh = q.transpose(0, 2, 1, 3)
    kh = k.transpose(0, 2, 1, 3)
    vh = v.transpose(0, 2, 1, 3)
    q_blocks = qh.reshape(B, H, nb, Q_BLOCK, dh).transpose(2, 0, 1, 3, 4)
    c_blocks = c.reshape(B, H, nb, Q_BLOCK).transpose(2, 0, 1, 3)
    k_pos = jnp.arange(S)
    scale = ATTN_HEAD_DIM ** -0.5

    def one_block(args):
        q_blk, c_blk, blk = args
        q_pos = blk * Q_BLOCK + jnp.arange(Q_BLOCK)
        s = jnp.einsum('bhqd,bhkd->bhqk', q_blk, kh, preferred_element_type=jnp.float32) * scale
        s = s + (c_blk[..., :, None] - c[..., None, :])
        s = jnp.where(k_pos[None, :] <= q_pos[:, None], s, -jnp.inf)
        p = jax.nn.softmax(s, axis=-1)
        return jnp.einsum('bhqk,bhkd->bhqd', p.astype(vh.dtype), vh)

    o = lax.map(one_block, (q_blocks, c_blocks, jnp.arange(nb)))
    return o.transpose(1, 0, 3, 2, 4).reshape(B, S, H * dh)

def chunked_spatial_gating(u, v, ln_gain, ln_bias, w_spatial, b_spatial):
    B, S, _ = v.shape
    vn = layer_norm(v, ln_gain, ln_bias)
    vc = vn.reshape(B, S // CHUNK, CHUNK, N_SGU_GROUPS, SGU_GROUP_DIM)
    causal = jnp.tril(jnp.ones((CHUNK, CHUNK), dtype=bool))
    w = jnp.where(causal[None], w_spatial, jnp.zeros_like(w_spatial))
    mixed = jnp.einsum('gts,bnsgc->bntgc', w, vc) + b_spatial.T[:, :, None]
    return u * mixed.reshape(B, S, SGU_WIDTH)

def setup_inputs(seed: int = 0) -> dict:
    key = jax.random.key(seed)
    ks = jax.random.split(key, 20)
    f32 = jnp.float32

    def nrm(k, shape, scale):
        return jax.random.normal(k, shape, f32) * scale

    L = DEPTH
    return {
        "x": nrm(ks[0], (BATCH, SEQ, D_MODEL), 1.0),
        "ffn1_norm": 1.0 + nrm(ks[1], (L, D_MODEL), 0.05),
        "ffn1_w_in": nrm(ks[2], (L, D_MODEL, 2 * D_FF), D_MODEL ** -0.5),
        "ffn1_w_out": nrm(ks[3], (L, D_FF, D_MODEL), D_FF ** -0.5),
        "mix_norm": 1.0 + nrm(ks[4], (L, D_MODEL), 0.05),
        "w_in": nrm(ks[5], (L, D_MODEL, IN_WIDTH), D_MODEL ** -0.5),
        "b_forget": FORGET_BIAS_OFFSET + nrm(ks[6], (L, N_ATTN_HEADS), 0.1),
        "b_gate": nrm(ks[7], (L, N_BRANCHES * D_MODEL), 0.1),
        "sgu_ln_gain": 1.0 + nrm(ks[8], (L, SGU_WIDTH), 0.05),
        "sgu_ln_bias": nrm(ks[9], (L, SGU_WIDTH), 0.05),
        "sgu_w_spatial": nrm(ks[10], (L, N_SGU_GROUPS, CHUNK, CHUNK), CHUNK ** -0.5),
        "sgu_b_spatial": 1.0 + nrm(ks[11], (L, N_SGU_GROUPS, CHUNK), 0.1),
        "w_up_attn": nrm(ks[12], (L, ATTN_WIDTH, D_MODEL), ATTN_WIDTH ** -0.5),
        "w_up_sgu": nrm(ks[13], (L, SGU_WIDTH, D_MODEL), SGU_WIDTH ** -0.5),
        "w_out": nrm(ks[14], (L, D_MODEL, D_MODEL), D_MODEL ** -0.5),
        "ffn2_norm": 1.0 + nrm(ks[15], (L, D_MODEL), 0.05),
        "ffn2_w_in": nrm(ks[16], (L, D_MODEL, 2 * D_FF), D_MODEL ** -0.5),
        "ffn2_w_out": nrm(ks[17], (L, D_FF, D_MODEL), D_FF ** -0.5),
        "final_norm": 1.0 + nrm(ks[18], (D_MODEL,), 0.05),
    }

def reference(x, ffn1_norm, ffn1_w_in, ffn1_w_out, mix_norm, w_in, b_forget, b_gate,
              sgu_ln_gain, sgu_ln_bias, sgu_w_spatial, sgu_b_spatial, w_up_attn, w_up_sgu,
              w_out, ffn2_norm, ffn2_w_in, ffn2_w_out, final_norm):
    B, S, _ = x.shape
    h = x
    for l in range(DEPTH):
        h = h + 0.5 * swiglu(rms_norm(h, ffn1_norm[l]), ffn1_w_in[l], ffn1_w_out[l])
        n = rms_norm(h, mix_norm[l])
        z = n @ w_in[l]
        q, k, v, f, u, vg, g = jnp.split(z, SPLIT_POINTS, axis=-1)
        hs = (B, S, N_ATTN_HEADS, ATTN_HEAD_DIM)
        attn = forgetting_attention(q.reshape(hs), k.reshape(hs), v.reshape(hs), f + b_forget[l])
        sgu = chunked_spatial_gating(jax.nn.gelu(u, approximate=False), jax.nn.gelu(vg, approximate=False),
                                     sgu_ln_gain[l], sgu_ln_bias[l], sgu_w_spatial[l], sgu_b_spatial[l])
        g_attn, g_sgu = jnp.split(jax.nn.sigmoid(g + b_gate[l]), 2, axis=-1)
        merged = g_attn * (attn @ w_up_attn[l]) + g_sgu * (sgu @ w_up_sgu[l])
        h = h + merged @ w_out[l]
        h = h + 0.5 * swiglu(rms_norm(h, ffn2_norm[l]), ffn2_w_in[l], ffn2_w_out[l])
    return rms_norm(h, final_norm)


_drawn_inputs = setup_inputs


def setup_inputs(seed=0):
    import zlib

    import numpy as np

    out = dict(_drawn_inputs(seed))
    spreads = {}
    factors = {'b_forget': 53.872,
     'b_gate': 3.461,
     'sgu_ln_gain': 5.337,
     'sgu_ln_bias': 5.196,
     'ffn2_norm': 3.132}
    for name, (base, spread) in spreads.items():
        noise = np.random.default_rng([zlib.crc32(name.encode()), seed]).standard_normal(out[name].shape)
        drawn = base * np.exp(spread * noise) if base else spread * noise
        out[name] = __import__('jax').numpy.asarray(drawn.astype(out[name].dtype))
    for name, factor in factors.items():
        out[name] = (out[name] * factor).astype(out[name].dtype)
    return out
```

```python
from contextlib import ExitStack

import concourse.bass as bass
from concourse import mybir

F32 = mybir.dt.float32
F32R = mybir.dt.float32r
BF16 = mybir.dt.bfloat16
ACT = mybir.ActivationFunctionType
ALU = mybir.AluOpType
AXX = mybir.AxisListType.X

P = 128
D = 1024
T = 512
KD = D // P
TB = T // P
FF = 2816
NF = FF // P
HEADS, DH = 8, 64
AW = HEADS * DH
KA = AW // P
GROUPS, GC = 8, 64
SW = GROUPS * GC
NG = 2 * D // P
RMS_EPS, LN_EPS = 1e-6, 1e-5
SCALE = DH ** -0.5
MASKED = -1e30

C_Q, C_K, C_V = 0, AW, 2 * AW
C_F = 3 * AW
C_U = C_F + HEADS
C_VG = C_U + SW
C_G = C_VG + SW

RING = 4
FIN_IT = NF // 2
FIN_U, FIN_P = 4 * FIN_IT, 2 * FIN_IT
FOUT_U, FOUT_P = NF, NF // 2
FFN_U, FFN_P = FIN_U + FOUT_U, FIN_P + FOUT_P
MIX_U, MIX_P = 52, 26
U_MIX, P_MIX = FFN_U, FFN_P
U_FFN = [0, FFN_U + MIX_U]
P_FFN = [0, FFN_P + MIX_P]
R_Q, R_K, R_V, R_VG, R_U, R_G, R_UA, R_UG, R_O = 0, 4, 8, 12, 16, 20, 36, 40, 44

S_FFN1, S_MIX, S_FFN2, S_FINAL = range(4)


def build(nc, x, ffn1_norm, ffn1_w_in, ffn1_w_out, mix_norm, w_in, b_forget, b_gate, sgu_ln_gain, sgu_ln_bias,
          sgu_w_spatial, sgu_b_spatial, w_up_attn, w_up_sgu, w_out, ffn2_norm, ffn2_w_in, ffn2_w_out, final_norm,
          out):
    ffn_w_in = [w[0].rearrange("(k p) n -> p k n", p=P) for w in (ffn1_w_in, ffn2_w_in)]
    ffn_w_out = [w[0].rearrange("(j p) n -> p j n", p=P) for w in (ffn1_w_out, ffn2_w_out)]
    mix_w_in = w_in[0].rearrange("(k p) n -> p k n", p=P)
    up_a = w_up_attn[0].rearrange("(k p) n -> p k n", p=P)
    up_g = w_up_sgu[0].rearrange("(k p) n -> p k n", p=P)
    w_o = w_out[0].rearrange("(k p) n -> p k n", p=P)

    ctx = ExitStack()
    with ctx:
        base = nc.sbuf_base + (-nc.sbuf_base) % 64
        arena = ctx.enter_context(nc.sbuf_tensor("arena", [P, (nc.sbuf_usable_end - base - 64) // 4], F32))
        used = [base]

        def at(name, shape, dt, offset):
            return nc.alloc_sbuf_tensor_at(name, shape, dt, offset=offset)

        def place(name, shape, dt=F32):
            size = (2 if dt == BF16 else 4)
            for n in shape[1:]:
                size *= n
            offset = used[0]
            used[0] += size + (-size) % 32
            return at(name, shape, dt, offset)

        h = place("h", [P, KD, T])
        xh = place("xh", [P, KD, T], F32R)
        xl = place("xl", [P, KD, T], F32R)
        raw = [place(f"raw{i}", [P, 2048]) for i in range(2)]
        wh = [place(f"wh{i}", [P, 1024], F32R) for i in range(RING)]
        wl = [place(f"wl{i}", [P, 1024], F32R) for i in range(RING)]
        work = [place(f"work{i}", [P, T]) for i in range(5)]
        squares = [work[3], work[4]]
        sqsum = place("sqsum", [P, T])
        rstd = place("rstd", [P, T])
        tri = place("tri", [P, T])
        ident = place("ident", [P, P])
        identb = place("identb", [P, P], BF16)
        maskb = place("maskb", [P, P], BF16)
        gains = place("gains", [P, 48])
        row0 = place("row0", [KD, P])
        rows = place("rows", [40, P])
        rtok = place("rtok", [P, TB])
        nv = place("nv", [P, TB])
        ny = place("ny", [P, TB])
        nt = place("nt", [P, TB])
        rowmax = place("rowmax", [P, 2])
        negmax = place("negmax", [P, 2])
        rowsum = place("rowsum", [P, 2])
        rowinv = place("rowinv", [P, 2])
        lnstat = place("lnstat", [P, TB, 6])
        lnmv = place("lnmv", [P, TB, 2])
        bforget = place("bforget", [HEADS, 1])
        lf_tok = place("lf_tok", [P, TB, HEADS])

        shared = used[0]
        kib = 1024
        act_h = at("act_h", [P, NF * T], F32R, shared)
        act_l = at("act_l", [P, NF * T], F32R, shared + NF * T * 4)
        x_in = at("x_in", [P, TB, D], F32, shared)
        y_feat = at("y_feat", [P, KD, T], F32, shared)
        y_tok = at("y_tok", [P, TB, D], F32, shared + 16 * kib)
        qa = at("qa", [P, HEADS, T], F32, shared)
        ka = at("ka", [P, HEADS, T], F32, shared + 16 * kib)
        attn_h = at("attn_h", [P, KA, T], F32R, shared)
        attn_l = at("attn_l", [P, KA, T], F32R, shared + 16 * kib)
        v_tok = at("v_tok", [P, TB, AW], F32, shared + 32 * kib)
        vn = at("vn", [P, TB, SW], F32, shared + 40 * kib)
        sgu_l = at("sgu_l", [P, KA, T], F32R, shared + 40 * kib)
        uT = at("uT", [P, KA, T], F32, shared + 48 * kib)
        sgu_h = at("sgu_h", [P, KA, T], F32R, shared + 48 * kib)
        wsT = at("wsT", [P, GROUPS, P], F32, shared + 56 * kib)
        gates = at("gates", [P, NG, T], F32, shared + 60 * kib)
        g0 = shared + 60 * kib
        wsp = at("wsp", [P, GROUPS, P], F32, g0)
        lng = at("lng", [P, SW], F32, g0 + 4 * kib)
        lnb = at("lnb", [P, SW], F32, g0 + 6 * kib)
        bsp = at("bsp", [P, KA, P], F32, g0 + 8 * kib)
        wf = at("wf", [P, KD, HEADS], F32, g0 + 10 * kib)
        wf_all = at("wf_all", [P, KD, P], F32R, g0 + 11 * kib)
        sgu_p = at("sgu_p", [P, KA, T], F32, g0 + 11 * kib)
        fz = [at(f"fz{i}", [HEADS, T], F32, g0 + (15 + 2 * i) * kib) for i in range(6)]
        vtmp = [at(f"vtmp{i}", [P, T], F32, g0 + (27 + 2 * i) * kib) for i in range(2)]
        assert shared + 92 * kib <= nc.sbuf_usable_end, (shared + 92 * kib, nc.sbuf_usable_end)

        bank = [ctx.enter_context(nc.psum_tensor(f"bank{i}", [P, 512], F32)) for i in range(8)]

        def sem(name):
            return ctx.enter_context(nc.semaphore(name))

        filler_ready = sem("filler_ready")
        x_loaded = [sem(f"x_loaded{t}") for t in range(TB)]
        row0_loaded = sem("row0_loaded")
        rows_loaded = sem("rows_loaded")
        first_loaded = [sem(f"first_loaded{i}") for i in range(2)]
        raw_loaded = [sem(f"raw_loaded{i}") for i in range(2)]
        hi_done = sem("hi_done")
        lo_done = sem("lo_done")
        unit_used = sem("unit_used")
        block_ready = sem("block_ready")
        h_done = sem("h_done")
        xh_done = sem("xh_done")
        xl_done = sem("xl_done")
        sq_done = sem("sq_done")
        sqsum_done = sem("sqsum_done")
        var_ready = sem("var_ready")
        inv_done = sem("inv_done")
        sqrt_done = sem("sqrt_done")
        rtok_done = sem("rtok_done")
        rbc_ready = sem("rbc_ready")
        rstd_done = sem("rstd_done")
        g_scaled = sem("g_scaled")
        u_scaled = sem("u_scaled")
        silu_done = sem("silu_done")
        a_done = sem("a_done")
        ah_done = sem("ah_done")
        al_done = sem("al_done")
        dve_step = sem("dve_step")
        act_step = sem("act_step")
        const_step = sem("const_step")
        gains_ready = sem("gains_ready")
        gains_done = sem("gains_done")
        qk_evac = sem("qk_evac")
        small_loaded = sem("small_loaded")
        wf_loaded = sem("wf_loaded")
        wf_zeroed = sem("wf_zeroed")
        wf_split = sem("wf_split")
        f_ready = sem("f_ready")
        f_logit = sem("f_logit")
        f_exp = sem("f_exp")
        f_ln = sem("f_ln")
        logf_done = sem("logf_done")
        logf_t_ready = sem("logf_t_ready")
        logf_t_done = sem("logf_t_done")
        c_ready = sem("c_ready")
        c_done = sem("c_done")
        ones_rows = sem("ones_rows")
        c_rows = sem("c_rows")
        v_evac = sem("v_evac")
        vg_evac = sem("vg_evac")
        vn_scaled = sem("vn_scaled")
        vn_done = sem("vn_done")
        vn_mid = sem("vn_mid")
        u_evac = sem("u_evac")
        u_gelu = sem("u_gelu")
        wsT_ready = sem("wsT_ready")
        wsT_done = sem("wsT_done")
        mix_ready = sem("mix_ready")
        mix_evac = sem("mix_evac")
        sgu_prod = sem("sgu_prod")
        sgu_h_done = sem("sgu_h_done")
        sgu_done = sem("sgu_done")
        s_ready = sem("s_ready")
        max_done = sem("max_done")
        exp_done = sem("exp_done")
        p_done = sem("p_done")
        pt_ready = sem("pt_ready")
        pt_evac = sem("pt_evac")
        pv_done = sem("pv_done")
        attn_h_done = sem("attn_h_done")
        attn_done = sem("attn_done")
        gate_evac = sem("gate_evac")
        sig_done = sem("sig_done")
        upa_ready = sem("upa_ready")
        upa_evac = sem("upa_evac")
        upg_ready = sem("upg_ready")
        upg_evac = sem("upg_evac")
        m_done = sem("m_done")
        mh_done = sem("mh_done")
        ml_done = sem("ml_done")
        y_done = sem("y_done")
        v4_done = sem("v4_done")
        yT_ready = sem("yT_ready")
        y0_evac = sem("y0_evac")
        y1_evac = sem("y1_evac")
        stored = sem("stored")

        BLOCKWISE = {U_FFN[0] + FFN_U - 1: (block_ready, KD * S_MIX + KD),
                     U_MIX + R_UG - 1: (upa_ready, KD),
                     U_MIX + R_O - 1: (upg_ready, KD),
                     U_MIX + MIX_U - 1: (block_ready, KD * S_FFN2 + KD),
                     U_FFN[1] + FFN_U - 1: (block_ready, KD * S_FINAL + KD)}

        def used(u):
            return u + 1 - sum(b <= u for b in BLOCKWISE)

        def wait_unit(engine, u):
            if u in BLOCKWISE:
                engine.wait_ge(*BLOCKWISE[u])
            else:
                engine.wait_ge(unit_used, used(u))

        def half_columns(slot, half):
            return raw[slot][:, :].rearrange("p (k n) -> p k n", k=KD)[:, :, half * P:(half + 1) * P]

        def half_rows(slot, half):
            return raw[slot][:, half * 1024:(half + 1) * 1024]

        def tiles(w):
            return w[:, :].rearrange("p (k n) -> p k n", k=KD)

        def mixer_source(r):
            p = P_MIX + r // 2
            columns = r < R_V or R_U <= r < R_UA
            part = half_columns if columns else half_rows
            return part(p % 2, r % 2), p % 2, p // 2 + 1, columns

        def ffn_out_source(e, n):
            p = P_FFN[e] + FIN_P + n // 2
            return half_rows(p % 2, n % 2), p % 2, p // 2 + 1, False

        def ffn_in_source(e, c):
            p = P_FFN[e] + c % 2
            return half_columns(p % 2, c // 2), p % 2, p // 2 + 1, True

        def split_hi(act, source, slot, loads):
            part, buf, count, columns = source
            if isinstance(loads, int) and loads == 0:
                act.wait_ge(first_loaded[buf], 16)
            else:
                act.wait_ge(raw_loaded[buf], loads * 16)
            dst = tiles(wh[slot]) if columns else wh[slot][:, :]
            nc.scalar.activation(dst, part, ACT.Copy).then_inc(hi_done, 1)

        def split_lo(dve, source, u, slot):
            part, buf, count, columns = source
            dve.wait_ge(hi_done, u + 1)
            hi = wh[slot][:, :].bitcast(F32)
            lo = wl[slot][:, :]
            if columns:
                hi = hi.rearrange("p (k n) -> p k n", k=KD)
                lo = lo.rearrange("p (k n) -> p k n", k=KD)
            nc.vector.tensor_tensor(lo, part, hi, ALU.subtract).then_inc(lo_done, 1)

        def source_of(u):
            for e in range(2):
                n = u - U_FFN[e]
                if 0 <= n < 4:
                    return ffn_in_source(e, n)
                if FIN_U <= n < FFN_U:
                    return ffn_out_source(e, n - FIN_U)
            return mixer_source(u - U_MIX)

        def hi_unit(act, u):
            source = source_of(u)
            if u >= RING:
                wait_unit(act, u - RING)
            split_hi(act, source, u % RING, 0 if u < 2 else source[2])

        def lo_unit(dve, u):
            split_lo(dve, source_of(u), u, u % RING)

        ITEMS = [(2 * b + half, i) for b in range(KA) for i in range(TB) for half in range(2)]
        N_ITEMS = len(ITEMS)

        block = ctx.enter_context(nc.Block())

        @block.sync
        def _(sp):
            for t in range(TB):
                sp.dma_start(x_in[:, t, :], x[0, t * P:(t + 1) * P, :]).then_inc(x_loaded[t], 16)

            def load(p, src, needs=None):
                if needs is not None:
                    sp.wait_ge(lo_done, needs)
                dst = raw[p % 2][:, :].rearrange("p (k n) -> p k n", k=src.shape[1])
                sp.dma_start(dst, src).then_inc(raw_loaded[p % 2], 16)

            def ffn(e):
                u0, p0 = U_FFN[e], P_FFN[e]
                w = ffn_w_in[e]
                if e == 0:
                    for half in range(2):
                        for i in range(2):
                            c0 = i * FF + half * P
                            sp.dma_start(half_columns(i, half), w[:, :, c0:c0 + P])\
                                .then_inc(raw_loaded[i] if half else first_loaded[i], 16)
                else:
                    load(p0, w[:, :, 0:256], u0 - 2)
                    load(p0 + 1, w[:, :, FF:FF + 256], u0)
                with sp.Fori(1, FIN_IT) as m:
                    load(p0, w[:, :, bass.ds(m * 256, 256)], m * 4 + (u0 - 1))
                    load(p0 + 1, w[:, :, bass.ds(m * 256 + FF, 256)], m * 4 + u0)
                w = ffn_w_out[e]
                u1, p1 = u0 + FIN_U, p0 + FIN_P
                load(p1, w[:, 0:2, :], u1 - 1)
                load(p1 + 1, w[:, 2:4, :], u1)
                with sp.Fori(1, FOUT_P // 2) as i:
                    load(p1, w[:, bass.ds(i * 4, 2), :], i * 4 + (u1 - 2))
                    load(p1 + 1, w[:, bass.ds(i * 4 + 2, 2), :], i * 4 + u1)
                load(p1 + FOUT_P - 1, w[:, NF - 2:NF, :], u1 + NF - 4)

            ffn(0)
            cols = lambda c, n: mix_w_in[:, :, c:c + n]
            pairs = [cols(C_Q, 256), cols(C_Q + 256, 256), cols(C_K, 256), cols(C_K + 256, 256),
                     mix_w_in[:, 0:4, C_V:C_V + AW], mix_w_in[:, 4:8, C_V:C_V + AW],
                     mix_w_in[:, 0:4, C_VG:C_VG + SW], mix_w_in[:, 4:8, C_VG:C_VG + SW],
                     cols(C_U, 256), cols(C_U + 256, 256)]
            pairs += [cols(C_G + 256 * g, 256) for g in range(8)]
            pairs += [w[:, 2 * k:2 * k + 2, :] for w in (up_a, up_g) for k in range(2)]
            pairs += [w_o[:, 2 * k:2 * k + 2, :] for k in range(4)]
            assert len(pairs) == MIX_P
            for n, src in enumerate(pairs):
                load(P_MIX + n, src, U_MIX + 2 * n - 2)
                if n == 9:
                    sp.wait_ge(c_done, 2)
                    sp.wait_ge(ones_rows, 2)
                    sp.wait_ge(qk_evac, 4)
                    for hd in range(HEADS):
                        sp.dma_start(qa[DH:DH + 1, hd, :], fz[4][hd:hd + 1, :]).then_inc(c_rows, 16)
                        sp.dma_start(ka[DH + 1:DH + 2, hd, :], fz[5][hd:hd + 1, :]).then_inc(c_rows, 16)
            ffn(1)
            for t in range(TB):
                sp.wait_ge(y0_evac, t + 1)
                sp.wait_ge(y1_evac, t + 1)
                sp.dma_start(out[0, t * P:(t + 1) * P, :], y_tok[:, t, :]).then_inc(stored, 16)
            sp.wait_ge(stored, 16 * TB)

        @block.gpsimd
        def _(pool):
            nc.gpsimd.memset(ident[:, :], 0.0).then_inc(const_step, 1)
            nc.gpsimd.memset(identb[:, :], 0.0).then_inc(const_step, 1)
            nc.gpsimd.memset(tri[:, :], 1.0).then_inc(const_step, 1)
            nc.gpsimd.memset(maskb[:, :], 0.0).then_inc(const_step, 1)
            pool.wait_ge(const_step, 4)
            for m in (ident, identb):
                nc.gpsimd.affine_select(out=m[:, :], in_=m[:, :], compare_op=ALU.not_equal, fill=1.0, base=0,
                                        pattern=[[-1, P]], channel_multiplier=1).then_inc(const_step, 1)
            nc.gpsimd.affine_select(out=tri[:, 0:P], in_=tri[:, 0:P], compare_op=ALU.is_ge, fill=0.0, base=0,
                                    pattern=[[1, P]], channel_multiplier=-1).then_inc(const_step, 1)
            nc.gpsimd.affine_select(out=maskb[:, :], in_=maskb[:, :], compare_op=ALU.is_ge, fill=MASKED, base=0,
                                    pattern=[[-1, P]], channel_multiplier=1).then_inc(const_step, 1)

            for n, (v, k) in enumerate(((mix_norm[0], 8), (ffn2_norm[0], 8), (final_norm, 8), (b_gate[0], 16))):
                pool.dma_start(rows[8 * n:8 * n + k, :], v.rearrange("(k p) -> k p", p=P)).then_inc(rows_loaded, 16)
            pool.dma_start(bforget[:, :], b_forget[0].rearrange("(h a) -> h a", a=1)).then_inc(rows_loaded, 16)

            def sum_squares(s):
                if s > 0:
                    pool.wait_ge(var_ready, s)
                for d in range(1, KD - 2 if s == S_FINAL else KD):
                    pool.wait_ge(sq_done, KD * s + d + 1)
                    if d > 1:
                        pool.wait_ge(sqsum_done, (KD - 1) * s + d - 1)
                    first = squares[0] if d == 1 else sqsum
                    nc.gpsimd.tensor_tensor(sqsum[:, :], first[:, :], squares[d % 2][:, :],
                                            ALU.add).then_inc(sqsum_done, 1)

            sum_squares(S_FFN1)
            sum_squares(S_MIX)
            pool.wait_ge(block_ready, KD * S_MIX + KD)
            pool.dma_start(wf[:, :, :], mix_w_in[:, :, C_F:C_F + HEADS]).then_inc(wf_loaded, 16)
            nc.gpsimd.memset(wf_all[:, :, :].bitcast(F32), 0.0).then_inc(wf_zeroed, 1)
            pool.dma_start(wsp[:, :, :], sgu_w_spatial[0].rearrange("g t s -> t g s")).then_inc(small_loaded, 16)
            pool.dma_start(lng[:, :], sgu_ln_gain[0:1, :].broadcast_to((P, SW))).then_inc(small_loaded, 16)
            pool.dma_start(lnb[:, :], sgu_ln_bias[0:1, :].broadcast_to((P, SW))).then_inc(small_loaded, 16)
            for g in range(GROUPS):
                half = (g % 2) * GC
                pool.dma_start(bsp[half:half + GC, g // 2, :],
                               sgu_b_spatial[0, g:g + 1, :].broadcast_to((GC, P))).then_inc(small_loaded, 16)
            pool.wait_ge(wf_zeroed, 1)
            nc.gpsimd.memset(qa[DH:96, :, :], 1.0).then_inc(ones_rows, 1)
            pool.wait_ge(ones_rows, 1)
            nc.gpsimd.memset(ka[DH:96, :, :], 1.0).then_inc(ones_rows, 1)
            pool.wait_ge(ones_rows, 2)
            pool.wait_ge(small_loaded, 16 * (3 + GROUPS))
            for t in range(TB):
                pool.wait_ge(vn_scaled, t + 1)
                nc.gpsimd.tensor_tensor(vtmp[t % 2][:, :], vn[:, t, :], lng[:, :], ALU.mult).then_inc(vn_mid, 1)
                pool.wait_ge(vn_mid, t + 1)
                nc.gpsimd.tensor_tensor(vn[:, t, :], vtmp[t % 2][:, :], lnb[:, :], ALU.add).then_inc(vn_done, 1)
            sum_squares(S_FFN2)
            sum_squares(S_FINAL)

        @block.scalar
        def _(act):
            def prepare(s, units={}):
                for d in range(KD):
                    if d in units:
                        hi_unit(act, units[d])
                    act.wait_ge(h_done, KD * s + d + 1)
                    gain = gains[:, KD * s + d:KD * s + d + 1]
                    if s == S_FFN2 and d == KD - 2:
                        act.wait_ge(block_ready, KD * s + KD)
                    if s != S_FINAL:
                        nc.scalar.activation(xh[:, d, :], h[:, d, :], ACT.Copy, scale=gain).then_inc(xh_done, 1)
                    if d >= 2:
                        act.wait_ge(sqsum_done, (KD - 1) * s + max(1, d - 2))
                    elif s > 0:
                        act.wait_ge(sqsum_done, (KD - 1) * s)
                    nc.scalar.activation(squares[d % 2][:, :], h[:, d, :], ACT.Square).then_inc(sq_done, 1)
                    if s == S_FINAL:
                        nc.scalar.activation(y_feat[:, d, :], h[:, d, :], ACT.Copy, scale=gain).then_inc(y_done, 1)

            def root(n):
                act.wait_ge(inv_done, n)
                nc.scalar.activation(ny[:, :], nt[:, :], ACT.Sqrt).then_inc(sqrt_done, 1)

            def ffn(e):
                s = 0 if e == 0 else 2
                u0 = U_FFN[e]
                hi_unit(act, u0 + 3)
                root(1 + s + (1 if e else 0))

                def body(m, ahead):
                    for jj in range(2):
                        n = (m * 2) + (NF * e + jj + 1)
                        act.wait_ge(g_scaled, n)
                        nc.scalar.activation(work[0][:, :], work[0][:, :], ACT.Silu).then_inc(silu_done, 1)
                        ahead(2 * jj)
                        ahead(2 * jj + 1)
                        act.wait_ge(a_done, n)
                        dst = act_h[:, bass.ds(m * (2 * T) + jj * T, T)]
                        nc.scalar.activation(dst, work[2][:, :], ACT.Copy).then_inc(ah_done, 1)

                with act.Fori(0, FIN_IT - 1) as m:
                    def ahead(c):
                        source = ffn_in_source(e, c)
                        act.wait_ge(unit_used, m * 4 + used(u0 + c))
                        split_hi(act, source, (u0 + c) % RING, m + (source[2] + 1))
                    body(m, ahead)
                body(FIN_IT - 1, lambda c: hi_unit(act, u0 + FIN_U + c))
                u1 = u0 + FIN_U
                with act.Fori(1, FOUT_U // 4) as i:
                    for c in range(4):
                        source = ffn_out_source(e, c)
                        act.wait_ge(unit_used, i * 4 + used(u1 + c - RING))
                        split_hi(act, source, (u1 + c) % RING, i + source[2])
                for n in range(FOUT_U // 4 * 4, FOUT_U):
                    hi_unit(act, u1 + n)

            act.dma_start(row0[:, :], ffn1_norm[0].rearrange("(k p) -> k p", p=P)).then_inc(row0_loaded, 16)
            act.wait_ge(const_step, 8)
            nc.scalar.activation(negmax[:, 0:1], ident[:, 0:1], ACT.Copy).then_inc(act_step, 1)
            act.wait_ge(gains_done, 1)
            prepare(S_FFN1, {0: 0, 1: 1, 7: 2})
            ffn(0)

            for r in range(2):
                hi_unit(act, U_MIX + r)
            prepare(S_MIX)
            hi_unit(act, U_MIX + 2)
            hi_unit(act, U_MIX + 3)
            root(2)
            for r in range(4, 8):
                hi_unit(act, U_MIX + r)
            act.wait_ge(f_logit, 1)
            nc.scalar.activation(fz[2][:, :], fz[1][:, :], ACT.Exp, scale=-1.0).then_inc(f_exp, 1)
            act.wait_ge(f_exp, 1)
            nc.scalar.activation(fz[3][:, :], fz[2][:, :], ACT.Ln, bias=1.0).then_inc(f_ln, 1)
            for r in range(8, 16):
                hi_unit(act, U_MIX + r)
            for t in range(TB):
                wait_unit(act, U_MIX + R_VG - 1)
                nc.scalar.activation(v_tok[:, t, :], bank[2 + t][:, :], ACT.Copy,
                                     scale=rtok[:, t:t + 1]).then_inc(v_evac, 1)
            for r in range(16, 20):
                hi_unit(act, U_MIX + r)
            VG_BANK = (0, 1, 6, 7)
            for t in range(TB):
                wait_unit(act, U_MIX + R_U - 1)
                nc.scalar.activation(vn[:, t, :], bank[VG_BANK[t]][:, :], ACT.Gelu,
                                     scale=rtok[:, t:t + 1]).then_inc(vg_evac, 1)
            root(3)
            for r in (20, 21):
                hi_unit(act, U_MIX + r)
            for b in range(KA):
                act.wait_ge(u_evac, b + 1)
                nc.scalar.activation(uT[:, b, :], uT[:, b, :], ACT.Gelu).then_inc(u_gelu, 1)

            def sgu_hi(b):
                act.wait_ge(sgu_prod, b + 1)
                nc.scalar.activation(sgu_h[:, b, :], sgu_p[:, b, :], ACT.Copy).then_inc(sgu_h_done, 1)

            def pt_copy(n):
                width = (ITEMS[n][1] + 1) * P
                act.wait_ge(pt_ready, n + 1)
                if n >= 2:
                    act.wait_ge(pv_done, n // 2)
                nc.scalar.activation(work[2 + n % 2][:, 0:width], bank[6 + n % 2][:, 0:width],
                                     ACT.Copy).then_inc(pt_evac, 1)

            def attn_hi(b):
                act.wait_ge(pv_done, TB * (b + 1))
                nc.scalar.activation(attn_h[:, b, :], bank[b % 2][:, :], ACT.Copy).then_inc(attn_h_done, 1)

            for n in range(N_ITEMS):
                width = (ITEMS[n][1] + 1) * P
                act.wait_ge(max_done, n + 1)
                nc.scalar.activation(work[n % 2][:, 0:width], bank[2 + n % 2][:, 0:width], ACT.Exp,
                                     bias=negmax[:, n % 2:n % 2 + 1], scale=SCALE,
                                     accum_out=rowsum[:, n % 2:n % 2 + 1]).then_inc(exp_done, 1)
                if n == 0:
                    for r in (22, 23):
                        hi_unit(act, U_MIX + r)
                if n >= 1:
                    pt_copy(n - 1)
                if 2 <= n < 2 + KA:
                    sgu_hi(n - 2)
                if n % 8 == 1 and n > 8:
                    attn_hi(n // 8 - 1)
                if n % 2 == 0 and n >= 2:
                    hi_unit(act, U_MIX + R_G + 4 + n // 2 - 1)
            pt_copy(N_ITEMS - 1)
            attn_hi(KA - 1)
            hi_unit(act, U_MIX + R_UA + 3)
            for g in range(NG):
                act.wait_ge(gate_evac, g + 1)
                nc.scalar.activation(gates[:, g, :], gates[:, g, :], ACT.Sigmoid,
                                     bias=gains[:, 32 + g:33 + g]).then_inc(sig_done, 1)
                if g in (3, 7):
                    hi_unit(act, U_MIX + R_UG + g // 4)
            for r in range(R_UG + 2, R_O + 2):
                hi_unit(act, U_MIX + r)
            for d in range(KD):
                act.wait_ge(m_done, d + 1)
                nc.scalar.activation(xh[:, d, :], gates[:, d, :], ACT.Copy).then_inc(mh_done, 1)
            for r in range(R_O + 2, MIX_U):
                hi_unit(act, U_MIX + r)
            for u in range(2):
                hi_unit(act, U_FFN[1] + u)
            prepare(S_FFN2)
            hi_unit(act, U_FFN[1] + 2)
            ffn(1)
            prepare(S_FINAL)
            root(5)
            act.wait_ge(rtok_done, 5)
            for t in range(TB):
                act.wait_ge(yT_ready, TB + t + 1)
                nc.scalar.activation(y_tok[:, t, T:D], bank[4 + t][:, :], ACT.Copy,
                                     scale=rtok[:, t:t + 1]).then_inc(y1_evac, 1)

        @block.vector
        def _(dve):
            step = [0]

            def link(ins):
                step[0] += 1
                ins.then_inc(dve_step, 1)
                dve.wait_ge(dve_step, step[0])

            def prepare(s):
                def lo(d):
                    dve.wait_ge(xh_done, KD * s + d + 1)
                    gain = gains[:, KD * s + d:KD * s + d + 1]
                    nc.vector.scalar_tensor_tensor(xl[:, d, :], h[:, d, :], gain, xh[:, d, :].bitcast(F32),
                                                   op0=ALU.mult, op1=ALU.subtract).then_inc(xl_done, 1)
                def residual(d):
                    dve.wait_ge(block_ready, KD * s + d + 1)
                    if s == S_FFN1:
                        nc.vector.tensor_copy(h[:, d, :], bank[d][:, :]).then_inc(h_done, 1)
                    else:
                        half = 1.0 if s == S_FFN2 else 0.5
                        nc.vector.scalar_tensor_tensor(h[:, d, :], bank[d][:, :], half, h[:, d, :],
                                                       op0=ALU.mult, op1=ALU.add).then_inc(h_done, 1)

                if s == S_FFN1:
                    residual(0)
                    residual(1)
                    lo_unit(dve, 0)
                    lo(0)
                    lo_unit(dve, 1)
                for d in range(2 if s == S_FFN1 else 0, KD):
                    residual(d)
                    if d >= 1 and s != S_FINAL:
                        lo(d - 1)
                if s != S_FINAL:
                    lo(KD - 1)
                    return
                for d in (KD - 2, KD - 1):
                    dve.wait_ge(sq_done, KD * s + d + 1)
                    dve.wait_ge(sqsum_done, (KD - 1) * s + d - 1)
                    nc.vector.tensor_tensor(sqsum[:, :], sqsum[:, :], squares[d % 2][:, :],
                                            ALU.add).then_inc(sqsum_done, 1)

            def rsqrt_tail(n):
                dve.wait_ge(sqrt_done, n)
                link(nc.vector.tensor_tensor(nt[:, :], ny[:, :], ny[:, :], ALU.mult))
                link(nc.vector.tensor_tensor(nt[:, :], nt[:, :], nv[:, :], ALU.mult))
                link(nc.vector.tensor_scalar(nt[:, :], nt[:, :], -0.5, 1.5, ALU.mult, ALU.add))
                nc.vector.tensor_tensor(rtok[:, :] if n != 3 else nv[:, :], ny[:, :], nt[:, :],
                                        ALU.mult).then_inc(rtok_done, 1)

            def token_rstd(s, n):
                dve.wait_ge(var_ready, s + 1)
                nc.vector.tensor_scalar(nv[:, :], bank[7][:, 0:TB], 1.0 / D, RMS_EPS, ALU.mult,
                                        ALU.add).then_inc(v4_done, 1)
                dve.wait_ge(v4_done, s + 1)
                nc.vector.reciprocal(nt[:, :], nv[:, :]).then_inc(inv_done, 1)
                rsqrt_tail(n)

            def row_rstd(s):
                dve.wait_ge(rbc_ready, s + 1)
                nc.vector.tensor_copy(rstd[:, :], bank[7][:, :]).then_inc(rstd_done, 1)
                dve.wait_ge(rstd_done, s + 1)

            def ffn(e):
                s = 0 if e == 0 else 2
                u0 = U_FFN[e]
                lo_unit(dve, u0 + 3)
                if e == 0:
                    dve.wait_ge(gains_ready, 2)
                    nc.vector.tensor_copy(gains[:, KD:48], bank[7][:, 0:40]).then_inc(gains_done, 1)
                token_rstd(s, 1 + s + (1 if e else 0))
                row_rstd(s)

                def body(m, ahead):
                    for jj in range(2):
                        n = (m * 2) + (NF * e + jj + 1)
                        dve.wait_ge(unit_used, m * 4 + used(u0 + 2 * jj + 1))
                        nc.vector.tensor_tensor(work[0][:, :], bank[2 * jj][:, :], rstd[:, :],
                                                ALU.mult).then_inc(g_scaled, 1)
                        nc.vector.tensor_tensor(work[1][:, :], bank[2 * jj + 1][:, :], rstd[:, :],
                                                ALU.mult).then_inc(u_scaled, 1)
                        ahead(2 * jj)
                        dve.wait_ge(u_scaled, n)
                        dve.wait_ge(silu_done, n)
                        nc.vector.tensor_tensor(work[2][:, :], work[0][:, :], work[1][:, :],
                                                ALU.mult).then_inc(a_done, 1)
                        ahead(2 * jj + 1)
                        dve.wait_ge(ah_done, n)
                        at_n = bass.ds(m * (2 * T) + jj * T, T)
                        nc.vector.tensor_tensor(act_l[:, at_n], work[2][:, :], act_h[:, at_n].bitcast(F32),
                                                ALU.subtract).then_inc(al_done, 1)

                with dve.Fori(0, FIN_IT - 1) as m:
                    body(m, lambda c: split_lo(dve, ffn_in_source(e, c), m * 4 + (u0 + 4 + c), (u0 + c) % RING))
                body(FIN_IT - 1, lambda c: lo_unit(dve, u0 + FIN_U + c))
                u1 = u0 + FIN_U
                with dve.Fori(1, FOUT_U // 4) as i:
                    for c in range(4):
                        split_lo(dve, ffn_out_source(e, c), i * 4 + (u1 + c), (u1 + c) % RING)
                for n in range(FOUT_U // 4 * 4, FOUT_U):
                    lo_unit(dve, u1 + n)

            nc.vector.memset(work[0][:, :], 0.0).then_inc(filler_ready, 1)
            dve.wait_ge(gains_ready, 1)
            nc.vector.tensor_copy(gains[:, 0:KD], bank[0][:, 0:KD]).then_inc(gains_done, 1)
            dve.wait_ge(gains_done, 1)
            prepare(S_FFN1)
            lo_unit(dve, 2)
            ffn(0)

            for r in range(2):
                lo_unit(dve, U_MIX + r)
            prepare(S_MIX)
            lo_unit(dve, U_MIX + 2)
            lo_unit(dve, U_MIX + 3)
            token_rstd(S_MIX, 2)
            for r in (4, 5):
                lo_unit(dve, U_MIX + r)
            row_rstd(S_MIX)
            dve.wait_ge(wf_loaded, 16)
            dve.wait_ge(wf_zeroed, 1)
            link(nc.vector.tensor_copy(wf_all[:, :, 0:HEADS], wf[:, :, :]))
            nc.vector.tensor_tensor(wf_all[:, :, 32:32 + HEADS], wf[:, :, :],
                                    wf_all[:, :, 0:HEADS].bitcast(F32), ALU.subtract).then_inc(wf_split, 1)

            def evac_duo(n, dst):
                wait_unit(dve, U_MIX + 2 * n + 1)
                b0 = 2 * (n % 3)
                for a in range(2):
                    for half in range(2):
                        lanes = slice(half * DH, half * DH + DH)
                        last = nc.vector.tensor_tensor(dst[0:DH, 4 * (n % 2) + 2 * a + half, :],
                                                       bank[b0 + a][lanes, :], rstd[lanes, :], ALU.mult)
                last.then_inc(qk_evac, 1)

            evac_duo(0, qa)
            for r in (6, 7):
                lo_unit(dve, U_MIX + r)
            evac_duo(1, qa)
            dve.wait_ge(f_ready, 1)
            link(nc.vector.tensor_copy(fz[0][:, :], bank[6][32:32 + HEADS, :]))
            link(nc.vector.tensor_tensor(fz[0][:, :], bank[6][0:HEADS, :], fz[0][:, :], ALU.add))
            link(nc.vector.tensor_tensor(fz[0][:, :], fz[0][:, :], rstd[0:HEADS, :], ALU.mult))
            link(nc.vector.tensor_scalar(fz[0][:, :], fz[0][:, :], bforget[:, 0:1], None, ALU.add))
            nc.vector.scalar_tensor_tensor(fz[1][:, :], fz[0][:, :], -1.0, fz[0][:, :],
                                           op0=ALU.mult, op1=ALU.max).then_inc(f_logit, 1)
            dve.wait_ge(f_ln, 1)
            nc.vector.scalar_tensor_tensor(fz[0][:, :], fz[0][:, :], 0.0, fz[3][:, :],
                                           op0=ALU.min, op1=ALU.subtract).then_inc(logf_done, 1)
            for r in (8, 9):
                lo_unit(dve, U_MIX + r)
            evac_duo(2, ka)
            dve.wait_ge(logf_t_ready, 1)
            nc.vector.tensor_copy(lf_tok[:, :, :], bank[6][:, 0:TB * HEADS].rearrange("p (j h) -> p j h", j=TB))\
                .then_inc(logf_t_done, 1)
            for r in (10, 11):
                lo_unit(dve, U_MIX + r)
            evac_duo(3, ka)
            dve.wait_ge(c_ready, 1)
            nc.vector.tensor_scalar(fz[4][:, :], bank[6][0:HEADS, :], 1.0 / SCALE, None, ALU.mult).then_inc(c_done, 1)
            nc.vector.tensor_scalar(fz[5][:, :], bank[6][0:HEADS, :], -1.0 / SCALE, None, ALU.mult).then_inc(c_done, 1)
            for r in range(12, 20):
                lo_unit(dve, U_MIX + r)
            for t in range(TB):
                dve.wait_ge(vg_evac, t + 1)
                link(nc.vector.bn_stats(lnstat[:, t, :], vn[:, t, :]))
                link(nc.vector.bn_aggr(lnmv[:, t, :], lnstat[:, t, :]))
            link(nc.vector.tensor_scalar(nv[:, :], lnmv[:, :, 1], LN_EPS, None, ALU.add))
            nc.vector.reciprocal(nt[:, :], nv[:, :]).then_inc(inv_done, 1)
            rsqrt_tail(3)
            dve.wait_ge(rtok_done, 3)
            for t in range(TB):
                nc.vector.tensor_scalar(vn[:, t, :], vn[:, t, :], lnmv[:, t, 0:1], nv[:, t:t + 1],
                                        ALU.subtract, ALU.mult).then_inc(vn_scaled, 1)
            for n in range(2):
                wait_unit(dve, U_MIX + R_U + 2 * n + 1)
                for a in range(2):
                    nc.vector.tensor_tensor(uT[:, 2 * n + a, :], bank[2 + 2 * n + a][:, :], rstd[:, :],
                                            ALU.mult).then_inc(u_evac, 1)
                if n == 0:
                    for half in range(2):
                        dve.wait_ge(wsT_ready, half + 1)
                        nc.vector.tensor_tensor(wsT[:, 4 * half:4 * half + 4, :],
                                                bank[half][:, :].rearrange("p (g t) -> p g t", g=4),
                                                tri[:, 0:P].unsqueeze(1).broadcast_to((P, 4, P)),
                                                ALU.mult).then_inc(wsT_done, 1)
                if n == 0:
                    for r in (20, 21):
                        lo_unit(dve, U_MIX + r)
            def sgu_product(b):
                dve.wait_ge(mix_ready, b + 1)
                dve.wait_ge(small_loaded, 16 * (3 + GROUPS))
                mixed = bank[(6, 7, 0, 1)[b]]
                nc.vector.tensor_tensor(sgu_p[:, b, :].rearrange("p (n t) -> p n t", n=TB),
                                        mixed[:, :].rearrange("p (n t) -> p n t", n=TB),
                                        bsp[:, b, :].unsqueeze(1).broadcast_to((P, TB, P)),
                                        ALU.add).then_inc(mix_evac, 1)
                dve.wait_ge(mix_evac, b + 1)
                dve.wait_ge(u_gelu, b + 1)
                nc.vector.tensor_tensor(sgu_p[:, b, :], sgu_p[:, b, :], uT[:, b, :], ALU.mult).then_inc(sgu_prod, 1)

            def sgu_lo(b):
                dve.wait_ge(sgu_h_done, b + 1)
                nc.vector.tensor_tensor(sgu_l[:, b, :], sgu_p[:, b, :], sgu_h[:, b, :].bitcast(F32),
                                        ALU.subtract).then_inc(sgu_done, 1)

            def attn_lo(b):
                dve.wait_ge(attn_h_done, b + 1)
                nc.vector.tensor_tensor(attn_l[:, b, :], bank[b % 2][:, :], attn_h[:, b, :].bitcast(F32),
                                        ALU.subtract).then_inc(attn_done, 1)

            for n in range(N_ITEMS):
                width = (ITEMS[n][1] + 1) * P
                i = n % 2
                dve.wait_ge(s_ready, n + 1)
                link(nc.vector.reduce_max(rowmax[:, i:i + 1], bank[2 + i][:, 0:width], axis=AXX))
                nc.vector.tensor_scalar(negmax[:, i:i + 1], rowmax[:, i:i + 1], -SCALE, None,
                                        ALU.mult).then_inc(max_done, 1)
                if i == 1 and n >= 3:
                    g = (n - 3) // 2
                    wait_unit(dve, U_MIX + R_G + g)
                    nc.vector.tensor_tensor(gates[:, g, :], bank[4 + g % 2][:, :], rstd[:, :],
                                            ALU.mult).then_inc(gate_evac, 1)
                    lo_unit(dve, U_MIX + R_G + 4 + g)
                if n == 0:
                    for b in range(KA):
                        sgu_product(b)
                dve.wait_ge(exp_done, n + 1)
                link(nc.vector.reciprocal(rowinv[:, i:i + 1], rowsum[:, i:i + 1]))
                nc.vector.tensor_scalar(work[i][:, 0:width], work[i][:, 0:width], rowinv[:, i:i + 1], None,
                                        ALU.mult).then_inc(p_done, 1)
                if n in (1, 2):
                    lo_unit(dve, U_MIX + 21 + n)
                if 3 <= n < 3 + KA:
                    sgu_lo(n - 3)
                if n % 8 == 2 and n > 8:
                    attn_lo(n // 8 - 1)
            wait_unit(dve, U_MIX + R_UA - 1)
            nc.vector.tensor_tensor(gates[:, NG - 1, :], bank[4 + (NG - 1) % 2][:, :], rstd[:, :],
                                    ALU.mult).then_inc(gate_evac, 1)
            lo_unit(dve, U_MIX + R_G + 4 + NG - 1)
            attn_lo(KA - 1)
            for r in (R_UG, R_UG + 1):
                lo_unit(dve, U_MIX + r)
            for d in range(KD):
                dve.wait_ge(upa_ready, d + 1)
                dve.wait_ge(sig_done, d + 1)
                nc.vector.tensor_tensor(gates[:, d, :], gates[:, d, :], bank[d][:, :], ALU.mult).then_inc(upa_evac, 1)
            for r in range(R_UG + 2, R_O + 2):
                lo_unit(dve, U_MIX + r)

            def merged_lo(d):
                dve.wait_ge(mh_done, d + 1)
                nc.vector.tensor_tensor(xl[:, d, :], gates[:, d, :], xh[:, d, :].bitcast(F32),
                                        ALU.subtract).then_inc(ml_done, 1)

            for d in range(KD):
                dve.wait_ge(upg_ready, d + 1)
                dve.wait_ge(sig_done, KD + d + 1)
                nc.vector.tensor_tensor(gates[:, KD + d, :], gates[:, KD + d, :], bank[d][:, :],
                                        ALU.mult).then_inc(upg_evac, 1)
                dve.wait_ge(upg_evac, d + 1)
                nc.vector.tensor_tensor(gates[:, d, :], gates[:, d, :], gates[:, KD + d, :],
                                        ALU.add).then_inc(m_done, 1)
                if d == 1:
                    merged_lo(0)
            for d in range(1, KD):
                merged_lo(d)
            for r in range(R_O + 2, MIX_U):
                lo_unit(dve, U_MIX + r)
            for u in range(2):
                lo_unit(dve, U_FFN[1] + u)
            prepare(S_FFN2)
            lo_unit(dve, U_FFN[1] + 2)
            ffn(1)
            prepare(S_FINAL)
            token_rstd(S_FINAL, 5)
            dve.wait_ge(rtok_done, 5)
            for t in range(TB):
                dve.wait_ge(yT_ready, t + 1)
                nc.vector.tensor_scalar(y_tok[:, t, 0:T], bank[t][:, :], rtok[:, t:t + 1], None,
                                        ALU.mult).then_inc(y0_evac, 1)

        @block.tensor
        def _(pe):
            def three(dst, sh, sl, mh, ml, start, stop):
                nc.tensor.matmul(dst, sh, mh, start=start, stop=False)
                nc.tensor.matmul(dst, sh, ml, start=False, stop=False)
                return nc.tensor.matmul(dst, sl, mh, start=False, stop=stop)

            def duo(u, slot, banks, s=None, hooks=()):
                for k in range(KD):
                    if s is not None:
                        pe.wait_ge(xl_done, KD * s + k + 1)
                    for i in range(2):
                        if k == 0:
                            pe.wait_ge(lo_done, u + (i + 1))
                        w = (slot + i) % RING
                        last = three(bank[banks[i]][:, :], wh[w][:, k * P:(k + 1) * P], wl[w][:, k * P:(k + 1) * P],
                                     xh[:, k, :], xl[:, k, :], k == 0, k == KD - 1)
                        if k == KD - 1:
                            last.then_inc(unit_used, 1)
                    for at_k, hook in hooks:
                        if at_k == k:
                            hook()

            def rows_unit(u, slot, mh, ml, start, order=range(KD), before=None):
                pe.wait_ge(lo_done, u + 1)
                for d in order:
                    if before is not None:
                        before(d)
                    last = three(bank[d][:, :], wh[slot][:, d * P:(d + 1) * P], wl[slot][:, d * P:(d + 1) * P],
                                 mh, ml, start, False)
                last.then_inc(unit_used, 1)

            def last_rows(u, mh, ml, done):
                pe.wait_ge(lo_done, u + 2)
                for d in range(KD):
                    for i in range(2):
                        w = (u + i) % RING
                        last = three(bank[d][:, :], wh[w][:, d * P:(d + 1) * P], wl[w][:, d * P:(d + 1) * P],
                                     mh[i], ml[i], False, i == 1)
                        if i == 1:
                            last.then_inc(done, 1)
                        elif d == KD - 1:
                            last.then_inc(unit_used, 1)

            def variance(s):
                pe.wait_ge(sqsum_done, (KD - 1) * (s + 1))
                pe.wait_ge(h_done, KD * s + KD)
                pe.wait_ge(gains_done, 2)
                for t in range(TB):
                    last = nc.tensor.matmul(bank[7][:, t:t + 1], sqsum[:, t * P:(t + 1) * P], tri[:, P:P + 1],
                                            start=True, stop=True)
                last.then_inc(var_ready, 1)

            def spread(n):
                pe.wait_ge(rtok_done, n)
                for t in range(TB):
                    last = nc.tensor.matmul(bank[7][:, t * P:(t + 1) * P], rtok[:, t:t + 1].broadcast_to((P, P)),
                                            ident[:, :], start=True, stop=True)
                last.then_inc(rbc_ready, 1)

            def other_gains():
                pe.wait_ge(rows_loaded, 16 * 5)
                pe.wait_ge(h_done, KD)
                nc.tensor.transpose(bank[7][:, 0:40], rows[:, :], ident[0:40, 0:40]).then_inc(gains_ready, 1)

            def ffn(e):
                s = S_FFN1 if e == 0 else S_FFN2
                u0 = U_FFN[e]
                u1 = u0 + FIN_U
                pe.wait_ge(h_done, KD * s + 2)
                if e == 0:
                    keep_warm(2)
                duo(u0, u0 % RING, (0, 1), s, ((KD - 1, other_gains),) if e == 0 else ())
                pe.wait_ge(h_done, KD * s + 4)
                duo(u0 + 2, (u0 + 2) % RING, (2, 3), None,
                    ((0, lambda: variance(s)), (2, lambda: spread(1 if e == 0 else 4))))
                with pe.Fori(1, FIN_IT) as m:
                    for jj in range(2):
                        pe.wait_ge(u_scaled, m * 2 + (NF * e + jj - 1))
                        duo(m * 4 + (u0 + 2 * jj), (u0 + 2 * jj) % RING, (2 * jj, 2 * jj + 1))

                def unit(n, slot, start=False, order=range(KD), before=None):
                    pe.wait_ge(al_done, n + (NF * e + 1))
                    rows_unit(n + u1, slot, act_h[:, bass.ds(n * T, T)], act_l[:, bass.ds(n * T, T)],
                              start, order, before)

                def bank_free(d):
                    if d == 0:
                        pe.wait_ge(u_scaled, NF * e + NF - 1)
                    elif d == 2:
                        pe.wait_ge(u_scaled, NF * e + NF)
                    elif d == 4:
                        pe.wait_ge(rstd_done, s + 1)

                unit(0, u1 % RING, True, (4, 5, 6, 7, 0, 1, 2, 3), bank_free)
                unit(1, (u1 + 1) % RING)
                with pe.Fori(0, (NF - 6) // 4) as i:
                    for c in range(4):
                        unit(i * 4 + (2 + c), (u1 + 2 + c) % RING)
                for n in range(NF - 4, NF - 2):
                    unit(n, (u1 + n) % RING)
                pe.wait_ge(al_done, NF * (e + 1))
                parts = [[a[:, n * T:(n + 1) * T] for n in (NF - 2, NF - 1)] for a in (act_h, act_l)]
                last_rows(u1 + NF - 2, *parts, block_ready)

            def keep_warm(n):
                for _ in range(n):
                    nc.tensor.matmul(bank[0][:, :], work[0][:, 0:P], work[0][:, :], start=True, stop=True)

            pe.wait_ge(filler_ready, 1)
            keep_warm(2)
            pe.wait_ge(row0_loaded, 16)
            pe.wait_ge(const_step, 8)
            nc.tensor.transpose(bank[0][:, 0:KD], row0[:, :], ident[0:KD, 0:KD]).then_inc(gains_ready, 1)
            pe.wait_ge(gains_done, 1)
            for t in range(TB):
                pe.wait_ge(x_loaded[t], 16)
                for d in range(KD):
                    last = nc.tensor.transpose(bank[d][:, t * P:(t + 1) * P], x_in[:, t, d * P:(d + 1) * P],
                                               ident[:, :])
                    if t == TB - 1:
                        last.then_inc(block_ready, 1)
            ffn(0)

            U = U_MIX
            pe.wait_ge(h_done, KD * S_MIX + 2)
            duo(U, U % RING, (0, 1), S_MIX)
            pe.wait_ge(h_done, KD * S_MIX + 4)
            duo(U + 2, (U + 2) % RING, (2, 3), None, ((0, lambda: variance(S_MIX)), (2, lambda: spread(2))))
            pe.wait_ge(wf_split, 1)
            for k in range(KD):
                nc.tensor.matmul(bank[6][:, :], wf_all[:, k, :], xh[:, k, :], start=(k == 0), stop=False)
                last = nc.tensor.matmul(bank[6][:, :], wf_all[:, k, :], xl[:, k, :], start=False, stop=(k == KD - 1))
            last.then_inc(f_ready, 1)
            duo(U + R_K, (U + R_K) % RING, (4, 5))

            def transpose_logf():
                pe.wait_ge(logf_done, 1)
                for t in range(TB):
                    last = nc.tensor.transpose(bank[6][:, t * HEADS:(t + 1) * HEADS], fz[0][:, t * P:(t + 1) * P],
                                               ident[0:HEADS, 0:HEADS])
                last.then_inc(logf_t_ready, 1)

            pe.wait_ge(qk_evac, 1)
            duo(U + R_K + 2, (U + R_K + 2) % RING, (0, 1), None, ((3, transpose_logf),))
            pe.wait_ge(logf_t_done, 1)
            for j in range(TB):
                last = nc.tensor.matmul(bank[6][0:HEADS, j * P:T], lf_tok[:, j, :], tri[:, 0:T - j * P],
                                        start=(j == 0), stop=(j == TB - 1))
            last.then_inc(c_ready, 1)

            def token_major(r, banks, before):
                for n in range(4):
                    u = U + r + n
                    w = u % RING
                    pe.wait_ge(lo_done, u + 1)
                    for t in range(TB):
                        if n == 0:
                            before(t)
                        for kk in range(2):
                            k = 2 * n + kk
                            mh, ml = (a[:, kk * T:(kk + 1) * T] for a in (wh[w], wl[w]))
                            tok = slice(t * P, (t + 1) * P)
                            last = three(bank[banks[t]][:, :], xh[:, k, tok], xl[:, k, tok], mh, ml,
                                         k == 0, k == KD - 1)
                    last.then_inc(unit_used, 1)

            def v_bank(t):
                if t in (0, 2):
                    pe.wait_ge(qk_evac, 2 + t // 2)

            def vg_bank(t):
                if t == 0:
                    pe.wait_ge(qk_evac, 4)
                elif t == 2:
                    pe.wait_ge(c_done, 2)
                elif t == 3:
                    pe.wait_ge(rstd_done, S_MIX + 1)

            token_major(R_V, (2, 3, 4, 5), v_bank)
            token_major(R_VG, (0, 1, 6, 7), vg_bank)

            def transpose_spatial():
                pe.wait_ge(small_loaded, 16 * (3 + GROUPS))
                pe.wait_ge(vg_evac, 2)
                for g in range(GROUPS):
                    last = nc.tensor.transpose(bank[g // 4][:, (g % 4) * P:(g % 4 + 1) * P], wsp[:, g, :],
                                               ident[:, :])
                    if g % 4 == 3:
                        last.then_inc(wsT_ready, 1)

            pe.wait_ge(v_evac, 2)
            duo(U + R_U, (U + R_U) % RING, (2, 3), None, ((5, transpose_spatial),))
            pe.wait_ge(v_evac, 4)
            duo(U + R_U + 2, (U + R_U + 2) % RING, (4, 5))

            def scores(n):
                hd, i = ITEMS[n]
                width = (i + 1) * P
                if n >= 2:
                    pe.wait_ge(exp_done, n - 1)
                dst = bank[2 + n % 2]
                nc.tensor.matmul(dst[:, 0:width], qa[0:DH + 2, hd, i * P:width], ka[0:DH + 2, hd, 0:width],
                                 start=True, stop=False)
                nc.tensor.matmul(dst[:, i * P:width], identb[:, :], maskb[:, :], start=False,
                                 stop=True).then_inc(s_ready, 1)

            def transposes(n):
                pe.wait_ge(p_done, n + 1)
                if n >= 2:
                    pe.wait_ge(pt_evac, n - 1)
                for j in range(ITEMS[n][1] + 1):
                    last = nc.tensor.transpose(bank[6 + n % 2][:, j * P:(j + 1) * P],
                                               work[n % 2][:, j * P:(j + 1) * P], ident[:, :])
                last.then_inc(pt_ready, 1)

            def values(pair):
                b, i = pair // TB, pair % TB
                pe.wait_ge(pt_evac, 2 * pair + 2)
                if i == 0 and b >= 2:
                    pe.wait_ge(attn_done, b - 1)
                for j in range(i + 1):
                    for half in range(2):
                        hd = 2 * b + half
                        last = nc.tensor.matmul(bank[b % 2][half * DH:(half + 1) * DH, i * P:(i + 1) * P],
                                                v_tok[:, j, hd * DH:(hd + 1) * DH],
                                                work[2 + half][:, j * P:(j + 1) * P],
                                                start=(j == 0), stop=(j == i))
                last.then_inc(pv_done, 1)

            def gate_half(n):
                g = n // 2
                u = U + R_G + g
                w = u % RING
                if n % 2 == 0:
                    pe.wait_ge(lo_done, u + 1)
                    if g >= 2:
                        pe.wait_ge(gate_evac, g - 1)
                for k in range(n % 2 * 4, n % 2 * 4 + 4):
                    last = three(bank[4 + g % 2][:, :], wh[w][:, k * P:(k + 1) * P], wl[w][:, k * P:(k + 1) * P],
                                 xh[:, k, :], xl[:, k, :], k == 0, k == KD - 1)
                if n % 2 == 1:
                    last.then_inc(unit_used, 1)

            pe.wait_ge(qk_evac, 4)
            pe.wait_ge(c_rows, 16 * 2 * HEADS)
            pe.wait_ge(v_evac, 4)
            pe.wait_ge(u_evac, 2)
            scores(0)

            pe.wait_ge(vn_done, TB)
            pe.wait_ge(wsT_done, 2)
            pe.wait_ge(vg_evac, 4)
            for b, bk in enumerate((6, 7, 0, 1)):
                for n in range(TB):
                    for half in range(2):
                        g = 2 * b + half
                        last = nc.tensor.matmul(bank[bk][half * GC:(half + 1) * GC, n * P:(n + 1) * P],
                                                vn[:, n, g * GC:(g + 1) * GC], wsT[:, g, :], start=True, stop=True)
                last.then_inc(mix_ready, 1)

            for n in range(N_ITEMS + 1):
                if 0 < n < N_ITEMS:
                    scores(n)
                if n == 1:
                    pe.wait_ge(u_evac, 4)
                    gate_half(0)
                    pe.wait_ge(mix_evac, 4)
                if n >= 1:
                    transposes(n - 1)
                if n >= 2:
                    gate_half(n - 1)
                if n >= 2 and n % 2 == 0:
                    values(n // 2 - 1)

            def upa_bank(d):
                if d in (4, 5):
                    pe.wait_ge(gate_evac, NG + d - 5)
                elif d == 2:
                    pe.wait_ge(exp_done, N_ITEMS)
                elif d == 6:
                    pe.wait_ge(pt_evac, N_ITEMS)
                elif d < 2:
                    pe.wait_ge(attn_done, 3 + d)

            def up(r, moving_h, moving_l, before, order, done):
                for k in range(KA - 2):
                    rows_unit(U + r + k, (U + r + k) % RING, moving_h[:, k, :], moving_l[:, k, :], k == 0,
                              order if k == 0 else range(KD), before if k == 0 else None)
                last_rows(U + r + KA - 2, *([a[:, k, :] for k in (KA - 2, KA - 1)] for a in (moving_h, moving_l)),
                          done)

            pe.wait_ge(attn_done, 2)
            up(R_UA, attn_h, attn_l, upa_bank, (2, 3, 6, 7, 4, 5, 0, 1), upa_ready)
            pe.wait_ge(sgu_done, KA)
            up(R_UG, sgu_h, sgu_l, lambda d: pe.wait_ge(upa_evac, d + 1), range(KD), upg_ready)
            for k in range(KD - 2):
                pe.wait_ge(ml_done, k + 1)
                rows_unit(U + R_O + k, (U + R_O + k) % RING, xh[:, k, :], xl[:, k, :], k == 0, range(KD),
                          (lambda d: pe.wait_ge(upg_evac, d + 1)) if k == 0 else None)
            pe.wait_ge(ml_done, KD)
            last_rows(U + R_O + KD - 2, *([a[:, k, :] for k in (KD - 2, KD - 1)] for a in (xh, xl)), block_ready)
            ffn(1)

            def back(half, t, d):
                return nc.tensor.transpose(bank[4 * half + t][:, (d % 4) * P:(d % 4 + 1) * P],
                                           y_feat[:, d, t * P:(t + 1) * P], ident[:, :])

            pe.wait_ge(h_done, KD * S_FINAL + 4)
            for d in range(4):
                pe.wait_ge(y_done, d + 1)
                for t in range(TB):
                    last = back(0, t, d)
                    if d == 3:
                        last.then_inc(yT_ready, 1)
            pe.wait_ge(h_done, KD * S_FINAL + KD)
            for d in range(4, KD):
                if d == KD - 1:
                    variance(S_FINAL)
                pe.wait_ge(y_done, d + 1)
                for t in range(3):
                    last = back(1, t, d)
                    if d == KD - 1:
                        last.then_inc(yT_ready, 1)
            pe.wait_ge(v4_done, S_FINAL + 1)
            for d in range(4, KD):
                last = back(1, 3, d)
            last.then_inc(yT_ready, 1)


_INS = ["x", "ffn1_norm", "ffn1_w_in", "ffn1_w_out", "mix_norm", "w_in", "b_forget", "b_gate", "sgu_ln_gain",
        "sgu_ln_bias", "sgu_w_spatial", "sgu_b_spatial", "w_up_attn", "w_up_sgu", "w_out", "ffn2_norm", "ffn2_w_in",
        "ffn2_w_out", "final_norm"]


def kernel(**inputs):
    import numpy as np
    import concourse.bacc as bacc
    from concourse.bass_utils import run_bass_kernel_spmd

    nc = bacc.Bacc("TRN2", target_bir_lowering=False, num_devices=1)
    arrays, args = {}, []
    for name in _INS:
        a = np.ascontiguousarray(inputs[name])
        arrays[f"in_{name}"] = a
        args.append(nc.dram_tensor(f"in_{name}", a.shape, mybir.dt.from_np(a.dtype), kind="ExternalInput").ap())
    args.append(nc.dram_tensor("out_h", (1, T, D), F32, kind="ExternalOutput").ap())
    build(nc, *args)
    r = run_bass_kernel_spmd(nc, [arrays], core_ids=[0])
    return r.results[0]["out_h"]
```
